# Optimizing a Trainium2 kernel written in Bass

```python
import math
import jax, jax.numpy as jnp
from jax import lax
import numpy as np

D_MODEL = 2048
BATCH = 1
SEQ = 512
DEPTH = 1

CHUNK = 64
Q_BLOCK = 128
FOX_HEADS = 8
FOX_HEAD_DIM = 128
GDN_HEADS = 8
GDN_HEAD_DIM = 128
GDN_CONV = 4
D_FF = 5632
FFN_CONV = 3
EPS = 1e-6

FOX_W = FOX_HEADS * FOX_HEAD_DIM
GDN_W = GDN_HEADS * GDN_HEAD_DIM
MIX_W = FOX_W + GDN_W
IN_SIZES = (3 * FOX_W, FOX_HEADS, 3 * GDN_W, GDN_HEADS, GDN_HEADS, GDN_W)
IN_COLS = 3 * FOX_W + FOX_HEADS + 4 * GDN_W + 2 * GDN_HEADS

kernel_name = "hybrid_fox_gdn_convffn_block"

def _split_at(x, sizes):
    idx, acc = [], 0
    for s in sizes[:-1]:
        acc += s
        idx.append(acc)
    return jnp.split(x, idx, axis=-1)

def rms_norm(x, gain):
    xf = x.astype(jnp.float32)
    y = xf * lax.rsqrt(jnp.mean(xf * xf, axis=-1, keepdims=True) + EPS)
    return (y * gain.astype(jnp.float32)).astype(x.dtype)

def l2_normalize(x):
    xf = x.astype(jnp.float32)
    return xf * lax.rsqrt(jnp.sum(xf * xf, axis=-1, keepdims=True) + EPS)

def modulate(h, shift, scale):
    return h * (1 + scale[:, None, :]) + shift[:, None, :]

def causal_dwconv(x, w, b=None):
    width, ch = w.shape
    y = lax.conv_general_dilated(
        x, w[:, None, :].astype(x.dtype), window_strides=(1,), padding=[(width - 1, 0)],
        dimension_numbers=("NWC", "WIO", "NWC"), feature_group_count=ch)
    return y if b is None else y + b.astype(x.dtype)

def forgetting_attention(q, k, v, f_logit, b_f):
    B, T, H, D = q.shape
    log_f = jax.nn.log_sigmoid(f_logit.astype(jnp.float32) + b_f.astype(jnp.float32))
    cum = jnp.cumsum(log_f, axis=1).transpose(0, 2, 1)
    scale = D ** -0.5
    outs = []
    for i in range(T // Q_BLOCK):
        q0, q1 = i * Q_BLOCK, (i + 1) * Q_BLOCK
        s = jnp.einsum("bqhd,bkhd->bhqk", q[:, q0:q1], k[:, :q1],
                       preferred_element_type=jnp.float32) * scale
        s = s + cum[:, :, q0:q1, None] - cum[:, :, None, :q1]
        causal = jnp.arange(q1)[None, :] <= jnp.arange(q0, q1)[:, None]
        p = jax.nn.softmax(jnp.where(causal, s, -jnp.inf), axis=-1)
        outs.append(jnp.einsum("bhqk,bkhd->bqhd", p.astype(v.dtype), v[:, :q1]))
    return jnp.concatenate(outs, axis=1)

def gated_delta_rule(q, k, v, g, beta):
    B, T, H, DK = q.shape
    DV = v.shape[-1]
    N = T // CHUNK
    q = q * DK ** -0.5

    def chunks(t):
        return t.reshape(B, N, CHUNK, H, *t.shape[3:]).swapaxes(2, 3)

    qc, kc, vc, bc = chunks(q), chunks(k), chunks(v), chunks(beta)
    gc = jnp.cumsum(chunks(g), axis=-1)
    tri_incl = jnp.tril(jnp.ones((CHUNK, CHUNK), bool))
    tri_strict = jnp.tril(jnp.ones((CHUNK, CHUNK), bool), -1)
    decay = jnp.exp(jnp.where(tri_incl, gc[..., :, None] - gc[..., None, :], -jnp.inf))

    k_beta = kc * bc[..., None]
    v_beta = vc * bc[..., None]
    low = jnp.where(tri_strict, jnp.einsum("bnhcd,bnhsd->bnhcs", k_beta, kc) * decay, 0.0)
    a_mat = low + jnp.eye(CHUNK, dtype=jnp.float32)
    rhs = jnp.concatenate([v_beta, k_beta * jnp.exp(gc)[..., None]], axis=-1)
    sol = lax.linalg.triangular_solve(a_mat, rhs, left_side=True, lower=True, unit_diagonal=True)
    u, w = sol[..., :DV], sol[..., DV:]

    attn = jnp.einsum("bnhcd,bnhsd->bnhcs", qc, kc) * decay
    q_dec = qc * jnp.exp(gc)[..., None]
    k_tail = kc * jnp.exp(gc[..., -1:] - gc)[..., None]
    g_last = jnp.exp(gc[..., -1])

    def step(state, inp):
        q_i, k_i, u_i, w_i, a_i, gl_i = inp
        v_new = u_i - jnp.einsum("bhck,bhkv->bhcv", w_i, state)
        o_i = (jnp.einsum("bhck,bhkv->bhcv", q_i, state)
               + jnp.einsum("bhcs,bhsv->bhcv", a_i, v_new))
        state = state * gl_i[..., None, None] + jnp.einsum("bhck,bhcv->bhkv", k_i, v_new)
        return state, o_i

    xs = tuple(jnp.moveaxis(t, 1, 0) for t in (q_dec, k_tail, u, w, attn, g_last))
    s0 = jnp.zeros((B, H, DK, DV), jnp.float32)
    _, o = lax.scan(step, s0, xs)
    return o.transpose(1, 0, 3, 2, 4).reshape(B, T, H, DV)

def hybrid_mixer(h, w_in, fox_forget_bias, fox_out_norm, gdn_conv_w, gdn_A_log, gdn_dt_bias,
                 gdn_out_norm, w_out):
    B, T, _ = h.shape
    proj = jnp.einsum("btd,de->bte", h, w_in)
    qkv_a, f_a, qkv_b, a_b, b_b, gate_b = _split_at(proj, IN_SIZES)

    qkv_a = qkv_a.reshape(B, T, 3, FOX_HEADS, FOX_HEAD_DIM)
    o_a = forgetting_attention(qkv_a[:, :, 0], qkv_a[:, :, 1], qkv_a[:, :, 2], f_a, fox_forget_bias)
    o_a = rms_norm(o_a, fox_out_norm).reshape(B, T, FOX_W)

    qkv_b = jax.nn.silu(causal_dwconv(qkv_b, gdn_conv_w)).reshape(B, T, 3, GDN_HEADS, GDN_HEAD_DIM)
    q_b = l2_normalize(qkv_b[:, :, 0])
    k_b = l2_normalize(qkv_b[:, :, 1])
    v_b = qkv_b[:, :, 2].astype(jnp.float32)
    beta = jax.nn.sigmoid(b_b.astype(jnp.float32))
    g = -jnp.exp(gdn_A_log.astype(jnp.float32)) * jax.nn.softplus(
        a_b.astype(jnp.float32) + gdn_dt_bias.astype(jnp.float32))
    o_b = gated_delta_rule(q_b, k_b, v_b, g, beta).astype(h.dtype)
    o_b = rms_norm(o_b, gdn_out_norm) * jax.nn.silu(gate_b.reshape(B, T, GDN_HEADS, GDN_HEAD_DIM))
    o_b = o_b.reshape(B, T, GDN_W)

    y = jnp.concatenate([o_a, o_b], axis=-1)
    return jnp.einsum("bte,ed->btd", y, w_out)

def conv_ffn(h, w_up, conv_w, conv_b, w_down):
    u = jnp.einsum("btd,df->btf", h, w_up)
    u = causal_dwconv(u, conv_w, conv_b)
    gate, val = jnp.split(u, 2, axis=-1)
    return jnp.einsum("btf,fd->btd", jax.nn.silu(gate) * val, w_down)

def setup_inputs(seed: int = 0) -> dict:
    key = jax.random.key(seed)
    ks = jax.random.split(key, 24)
    f32 = jnp.float32

    def nrm(k, shape, s):
        return s * jax.random.normal(k, shape, f32)

    def gain(k, n):
        return 1.0 + 0.05 * jax.random.normal(k, (DEPTH, n), f32)

    dt = jnp.exp(jax.random.uniform(ks[10], (DEPTH, GDN_HEADS), f32,
                                    minval=math.log(1e-3), maxval=math.log(1e-1)))
    return {
        "x": nrm(ks[0], (BATCH, SEQ, D_MODEL), 1.0),
        "c": nrm(ks[1], (BATCH, D_MODEL), 1.0),
        "w_ada": nrm(ks[2], (DEPTH, D_MODEL, 6 * D_MODEL), D_MODEL ** -0.5),
        "b_ada": nrm(ks[3], (DEPTH, 6 * D_MODEL), 0.02),
        "norm_mix_pre": gain(ks[4], D_MODEL),
        "norm_mix_post": gain(ks[5], D_MODEL),
        "w_in": nrm(ks[6], (DEPTH, D_MODEL, IN_COLS), D_MODEL ** -0.5),
        "fox_forget_bias": jax.random.uniform(ks[7], (DEPTH, FOX_HEADS), f32, minval=1.0, maxval=5.0),
        "fox_out_norm": gain(ks[8], FOX_HEAD_DIM),
        "gdn_conv_w": nrm(ks[9], (DEPTH, GDN_CONV, 3 * GDN_W), GDN_CONV ** -0.5),
        "gdn_A_log": jnp.log(jax.random.uniform(ks[11], (DEPTH, GDN_HEADS), f32, minval=1.0, maxval=16.0)),
        "gdn_dt_bias": dt + jnp.log(-jnp.expm1(-dt)),
        "gdn_out_norm": gain(ks[12], GDN_HEAD_DIM),
        "w_out": nrm(ks[13], (DEPTH, MIX_W, D_MODEL), MIX_W ** -0.5),
        "norm_ffn_pre": gain(ks[14], D_MODEL),
        "norm_ffn_post": gain(ks[15], D_MODEL),
        "w_up": nrm(ks[16], (DEPTH, D_MODEL, 2 * D_FF), D_MODEL ** -0.5),
        "ffn_conv_w": nrm(ks[17], (DEPTH, FFN_CONV, 2 * D_FF), FFN_CONV ** -0.5),
        "ffn_conv_b": nrm(ks[18], (DEPTH, 2 * D_FF), 0.02),
        "w_down": nrm(ks[19], (DEPTH, D_FF, D_MODEL), D_FF ** -0.5),
    }

def reference(x, c, w_ada, b_ada, norm_mix_pre, norm_mix_post, w_in, fox_forget_bias, fox_out_norm,
              gdn_conv_w, gdn_A_log, gdn_dt_bias, gdn_out_norm, w_out, norm_ffn_pre, norm_ffn_post,
              w_up, ffn_conv_w, ffn_conv_b, w_down):
    cond = jax.nn.silu(c)
    for l in range(DEPTH):
        mod = jnp.einsum("bd,de->be", cond, w_ada[l]) + b_ada[l]
        sh_m, sc_m, ga_m, sh_f, sc_f, ga_f = jnp.split(mod, 6, axis=-1)

        h = modulate(rms_norm(x, norm_mix_pre[l]), sh_m, sc_m)
        y = hybrid_mixer(h, w_in[l], fox_forget_bias[l], fox_out_norm[l], gdn_conv_w[l], gdn_A_log[l],
                         gdn_dt_bias[l], gdn_out_norm[l], w_out[l])
        x = x + ga_m[:, None, :] * rms_norm(y, norm_mix_post[l])

        h = modulate(rms_norm(x, norm_ffn_pre[l]), sh_f, sc_f)
        y = conv_ffn(h, w_up[l], ffn_conv_w[l], ffn_conv_b[l], w_down[l])
        x = x + ga_f[:, None, :] * rms_norm(y, norm_ffn_post[l])
    return x


_drawn_inputs = setup_inputs


def setup_inputs(seed=0):
    import zlib

    import numpy as np

    out = dict(_drawn_inputs(seed))
    spreads = {}
    factors = {'gdn_out_norm': 3.521, 'ffn_conv_b': 5.917}
    for name, (base, spread) in spreads.items():
        noise = np.random.default_rng([zlib.crc32(name.encode()), seed]).standard_normal(out[name].shape)
        drawn = base * np.exp(spread * noise) if base else spread * noise
        out[name] = __import__('jax').numpy.asarray(drawn.astype(out[name].dtype))
    for name, factor in factors.items():
        out[name] = (out[name] * factor).astype(out[name].dtype)
    return out
```

```python
from contextlib import ExitStack

import numpy as np

import concourse.bass as bass
from concourse import mybir

F32 = mybir.dt.float32
F32R = mybir.dt.float32r
ACT = mybir.ActivationFunctionType
ALU = mybir.AluOpType
AX = mybir.AxisListType

P = 128
T = 512
D = 2048
KB = D // P
NH = 8
HD = 128
FF = 5632
FB = FF // P
GRP = 4
FOX_COLS = 3 * NH * HD
GDN_COL0 = FOX_COLS + NH
AB_COL0 = GDN_COL0 + 3 * NH * HD
GATE_COL0 = AB_COL0 + 2 * NH
CONV, FCONV = 4, 3
EPS = 1e-6
QSCALE = HD ** -0.5
NEG = -1e30
CK = 128
NCK = T // CK
LEVELS = [2, 4, 8, 16, 32, 64]
NL = len(LEVELS)

U_FAB = 0
U_GATE_A = 1
U_GDN_A = 3
U_GATE_B = 15
U_STEP0 = 16
U_GATE_C = 28
U_STEP1 = 29
U_FOXA = 41
U_FOXB = 53
U_OUT = 57
U_FFN = 73
N_UNITS = U_FFN + 12 * (FB // GRP)

C_ID, C_ONE, C_INC, C_STR, C_NEG, C_ML1, C_MU = 0, 128, 256, 384, 512, 640, 768
C_EPS = C_MU + 128 * 7
N_CONST = C_EPS + 2

V_BADA, V_C = 0, 96
V_GCONV, V_MIXPRE, V_FOXN, V_GDNN = 128, 224, 240, 241
V_FCONV = 256
V_MIXPOST, V_FFNPRE, V_FFNPOST = 352, 480, 608


class Idx:

    def __init__(self, base, stride=0, reg=None):
        if isinstance(reg, int):
            base, stride, reg = base + stride * reg, 0, None
        self.base, self.stride, self.reg = base, stride, reg

    def __add__(self, k):
        return Idx(self.base + k, self.stride, self.reg)

    def __mul__(self, k):
        return Idx(self.base * k, self.stride * k, self.reg)

    def __floordiv__(self, k):
        assert self.stride % k == 0
        return Idx(self.base // k, self.stride // k, self.reg)

    def __mod__(self, k):
        assert self.stride % k == 0
        return self.base % k

    @property
    def v(self):
        return self.base if self.reg is None or self.stride == 0 else self.reg * self.stride + self.base


class Chain:

    def __init__(self, eng, sem):
        self.eng, self.sem, self.at = eng, sem, Idx(0)

    def __call__(self, ins):
        self.at = self.at + 1
        ins.then_inc(self.sem, 1)
        self.eng.wait_ge(self.sem, self.at.v)

    def loop(self, reg, per):
        self.base, self.per = self.at.base, per
        self.at = Idx(self.base, per, reg)

    def end(self, times):
        got = self.at.base - self.base
        assert got == self.per, f"{self.sem}: the body counts {got}, not {self.per}"
        self.at = Idx(self.base + self.per * times)


def heads(tile):
    return tile.rearrange("p (h c) -> p h c", h=GRP)


def over_heads(mask):
    return mask.unsqueeze(1).to_broadcast([P, GRP, P])


def over_free(cols):
    return cols.unsqueeze(2).to_broadcast([P, GRP, P])


def build(nc, I, consts, out):
    qkv_d = nc.dram_tensor("qkv_scratch", (2, NH, 3, P, T), F32, kind="Internal").ap()
    gate_d = nc.dram_tensor("gate_scratch", (NH, P, T), F32, kind="Internal").ap()
    y_d = nc.dram_tensor("y_scratch", (KB, P, T), F32, kind="Internal").ap()
    rows_d = nc.dram_tensor("rows_scratch", (2 * NH, T), F32, kind="Internal").ap()
    sct_d = nc.dram_tensor("scalars_scratch", (2, NCK, P, 20), F32, kind="Internal").ap()
    w_ada, w_in, w_out, w_up, w_down = (I[k][0] for k in ("w_ada", "w_in", "w_out", "w_up", "w_down"))

    ctx = ExitStack()
    with ctx:
        def sb(name, cols, dt=F32, where=None):
            return (where or ctx).enter_context(nc.sbuf_tensor(name, [P, cols], dt))

        def sem(name):
            return ctx.enter_context(nc.semaphore(name))

        x_hi = sb("x_hi", KB * T, F32R)
        x_lo = sb("x_lo", KB * T, F32R)
        raw = sb("raw", 2 * 2048)
        w_hi = sb("w_hi", 4 * 1024, F32R)
        w_lo = sb("w_lo", 4 * 1024, F32R)
        vec = sb("vec", 768)
        mod = sb("mod", 96)
        cond = sb("cond", KB)
        s_mix, s_ffn, g_mix, g_ffn = (sb(n, KB) for n in ("s_mix", "s_ffn", "g_mix", "g_ffn"))
        idone = sb("idone", 2 * P)
        ident, ones = idone[:, 0:P], idone[:, P:2 * P]
        eps = sb("eps", 2)
        ph0 = ExitStack()
        x_tok = sb("x_tok", 2 * D, F32, ph0)
        xnT = sb("xnT", KB * T, F32, ph0)
        adw0 = sb("adw0", 2 * 2048, F32, ph0)
        ada_acc0 = sb("ada_acc0", 512, F32, ph0)
        rows_in = sb("rows_in", 768, F32, ph0)
        rstd0 = sb("rstd0", 8, F32, ph0)
        junk0 = sb("junk0", D, F32, ph0)
        ph0.close()
        ph1 = ExitStack()
        guard = sb("guard", 4096, F32, ph1)
        adw1 = guard
        ada_acc1 = sb("ada_acc1", 512, F32, ph1)
        kqv = [sb(f"kqv{b}", 3 * 512, F32, ph1) for b in range(2)]
        gcb = [sb(f"gcb{b}", 512, F32, ph1) for b in range(2)]
        sct = [sb(f"sct{b}", 20, F32, ph1) for b in range(2)]
        wk = sb("work", 17 * 512, F32, ph1)
        pre = sb("pre", 3 + T, F32, ph1)
        act_t = sb("act_t", T, F32, ph1)
        sq_t = sb("sq_t", T, F32, ph1)
        fin = [sb(f"fin{b}", T, F32, ph1) for b in range(2)]
        oT = sb("oT", 512, F32, ph1)
        st1 = sb("st1", 32, F32, ph1)
        cst = sb("cst", N_CONST - 2 * P - 2, F32, ph1)
        cw = sb("cw", 12, F32, ph1)
        hb = sb("hb", 32, F32, ph1)
        ph1.close()
        ph2 = ExitStack()
        accT = sb("accT", KB * T, F32, ph2)
        x1T = sb("x1T", KB * T, F32, ph2)
        ph2a = ExitStack()
        hid_hi = sb("hid_hi", GRP * T, F32R, ph2a)
        hid_lo = sb("hid_lo", GRP * T, F32R, ph2a)
        ph2a.close()
        ph2b = ExitStack()
        y_in = [sb(f"y_in{b}", T, F32, ph2b) for b in range(2)]
        g_in = [sb(f"g_in{b}", T, F32, ph2b) for b in range(2)]
        x_blk = [sb(f"x_blk{b}", T, F32, ph2b) for b in range(2)]
        sqs = [sb(f"sqs{b}", T, F32, ph2b) for b in range(2)]
        ph2b.close()
        ph2c = ExitStack()
        o_tok = [sb(f"o_tok{b}", T, F32, ph2c) for b in range(2)]
        ph2c.close()
        ph2d = ExitStack()
        sb("hid_place", 2 * GRP * T, F32, ph2d)
        fpre = sb("fpre", 2 + T, F32, ph2d)
        g_t = sb("g_t", T, F32, ph2d)
        v_t = sb("v_t", T, F32, ph2d)
        fcw = sb("fcw", 32, F32, ph2d)
        osq = [fpre[:, 0:T], g_t[:, :]]
        ph2d.close()
        ph2.close()

        acc = [ctx.enter_context(nc.psum_tensor(f"acc{b}", [P, T], F32)) for b in range(2)]
        nb = ctx.enter_context(nc.psum_tensor("nb", [P, T], F32))
        G = [ctx.enter_context(nc.psum_tensor(f"G{b}", [P, T], F32)) for b in range(5)]

        def w(k, n=1):
            return wk[:, k * 512:(k + n) * 512]
        D_t, BM_t, ta_t, Up_t, at_t = w(0), w(1), w(2), w(3), w(4)
        Upb = [w(5), w(6)]
        Ys_t, X_t, XT_t, R_t, kt_t, vn_t, vnt_t, S_t, o_t, so_t = (w(k) for k in range(7, 17))
        P_t = wk[:, 0:1280]
        PT_t = wk[:, 1280:2560]
        vtok_t = w(10)
        POFF = [0, 128, 384, 768]

        def cs(c, n=P):
            return cst[:, c - 2 * P:c - 2 * P + n]

        names = """raw_landed0 raw_landed1 fab_in hi_ready lo_ready piece_used acc_evac
            const_in vecrows_in x_in cleared vec_t vec_ready cond_ready x_scaled xt_done xn_ready
            ada_landed0 ada_landed1 ada_used ada_acc_ready ada_sum_done h_tmp h_hi_done h_ready
            cst_in fab_t fab_k fab_e1 fab_dve fab_act fab_lg fab_cum rows_t rows_ready scal_ready fab_stored
            conv_ready sq_ready ssq_done rs_ready mul_ready stored0 stored1
            step_in0 step_in1 step_free bm_ready dif_ready d_ready scores_done tok_done tok_evac
            ks_done qs_done up_ready attn_ready lt_done x_ready upb_ready y_done ys_ready z_done
            xt_final xr_done vn_ready vnt_ready av_done kv_done s_decayed state_ready
            o_ready so_ready oss_ready orr_ready on_ready ot_done ot_evac y_stored
            fox_v_done fox_vt_ready fox_s_done fox_m_ready fox_p_ready fox_pt_done fox_pt_ready fox_pv_done
            yld0 yld1 gld0 gld1 y_mul y_hi y_split
            xb_in0 xb_in1 xb_t xb_ready sq_out ssum_ready nsum_done r_ready x1_ready xsq_ready nsum2_done
            r2_ready h2_tmp h2_hi h2_ready acc_zero
            fconv_ready silu_ready hidden_tmp hidden_hi hidden_ready down_done acc_added
            osq_ready nsum3_done r3_ready fin_x out_t out_evac out_stored0 out_stored1
            dve_chain act_chain""".split()
        S = {n: sem(n) for n in names}
        raw_landed = [S["raw_landed0"], S["raw_landed1"]]
        stored = [S["stored0"], S["stored1"]]
        step_in = [S["step_in0"], S["step_in1"]]
        ada_landed = [S["ada_landed0"], S["ada_landed1"]]
        yld, gld, xb_in = ([S[n + b] for b in "01"] for n in ("yld", "gld", "xb_in"))
        out_stored = [S["out_stored0"], S["out_stored1"]]

        def piece_at(tile, piece):
            return tile[:, (piece % 4) * 1024:(piece % 4 + 1) * 1024]

        def landed(u):
            return (u // 2 + u % 2) * 16

        def stores_before(f):
            return (f // 2) * 16

        def xs(tile, k):
            return tile[:, k * T:(k + 1) * T]

        def mask(c):
            return over_heads(cs(c))

        block = ctx.enter_context(nc.Block())

        @block.sync
        def _(sp):
            def wait(s, count):
                sp.wait_ge(s, count.v)

            def load_unit(u, src, blocks=KB):
                if u.base >= 2:
                    wait(S["lo_ready"], u * 2 + -2)
                dst = raw[:, (u % 2) * 2048:(u % 2 + 1) * 2048].rearrange("p (k c) -> p k c", k=blocks)
                sp.dma_start(dst, src.rearrange("(k p) c -> p k c", p=P)).then_inc(raw_landed[u % 2], 16)

            def in_cols(col0, head):
                return w_in[:, bass.ds((head * P + col0).v, P)]

            def load_ada(sl, k4, tile):
                q = sl * 4 + k4
                if q.base >= 2:
                    wait(S["ada_used"], q + -1)
                sp.dma_start(tile[:, (q % 2) * 2048:(q % 2 + 1) * 2048].rearrange("p (k c) -> p k c", k=4),
                             w_ada[k4 * 512:(k4 + 1) * 512, bass.ds((sl * 512).v, 512)]
                             .rearrange("(k p) c -> p k c", p=P)).then_inc(ada_landed[q % 2], 16)

            sp.dma_start(idone[:, :], consts[:, 0:2 * P]).then_inc(S["const_in"], 16)
            sp.dma_start(eps[:, :], consts[:, C_EPS:C_EPS + 2]).then_inc(S["const_in"], 16)
            sp.wait_ge(S["cleared"], 2)
            fw = I["ffn_conv_w"][0]
            for rows, col, src in [
                    (0, V_BADA, I["b_ada"][0].rearrange("(r c) -> r c", c=P)),
                    (96, V_BADA, I["c"][0].rearrange("(r c) -> r c", c=P)),
                    (0, V_GCONV, I["gdn_conv_w"][0].rearrange("j (r c) -> (j r) c", c=P)),
                    (96, V_GCONV, I["norm_mix_pre"][0].rearrange("(r c) -> r c", c=P)),
                    (112, V_GCONV, I["fox_out_norm"]), (113, V_GCONV, I["gdn_out_norm"]),
                    (0, V_FCONV, fw[0].rearrange("(r c) -> r c", c=P)),
                    (0, V_FCONV + P, fw[1].rearrange("(r c) -> r c", c=P)),
                    (0, V_FCONV + 2 * P, fw[2].rearrange("(r c) -> r c", c=P)),
                    (0, V_FCONV + 3 * P, I["ffn_conv_b"][0].rearrange("(r c) -> r c", c=P)),
                    (96, V_FCONV, I["norm_mix_post"][0].rearrange("(r c) -> r c", c=P)),
                    (96, V_FCONV + P, I["norm_ffn_pre"][0].rearrange("(r c) -> r c", c=P)),
                    (96, V_FCONV + 2 * P, I["norm_ffn_post"][0].rearrange("(r c) -> r c", c=P))]:
                sp.dma_start(rows_in[rows:rows + src.shape[0], col:col + P], src).then_inc(S["vecrows_in"], 16)
            for b in range(2):
                sp.dma_start(x_tok[:, b * D:(b + 1) * D], I["x"][0, b * P:(b + 1) * P, :]).then_inc(S["x_in"], 16)
                sp.wait_ge(S["x_in"], 16 * (b + 1))
            for k4 in range(4):
                load_ada(Idx(0), k4, adw0)
            with sp.Fori(0, 7) as i:
                for k4 in range(4):
                    load_ada(Idx(1, 1, i), k4, adw0)
            r0 = raw[:, 0:2048].rearrange("p (k c) -> p k c", k=KB)
            sp.dma_start(r0[:, :, 0:NH], w_in[:, FOX_COLS:FOX_COLS + NH].rearrange("(k p) c -> p k c", p=P))\
              .then_inc(S["fab_in"], 16)
            sp.dma_start(r0[:, :, NH:3 * NH], w_in[:, AB_COL0:AB_COL0 + 2 * NH].rearrange("(k p) c -> p k c", p=P))\
              .then_inc(S["fab_in"], 16)
            load_unit(Idx(1), in_cols(GATE_COL0, Idx(0)))
            sp.wait_ge(S["h_ready"], KB)
            sp.dma_start(cst[:, :], consts[:, 2 * P:C_EPS]).then_inc(S["cst_in"], 16)
            for k, name in enumerate(("fox_forget_bias", "gdn_dt_bias", "gdn_A_log")):
                sp.dma_start(hb[:, k * NH:(k + 1) * NH], I[name].to_broadcast([P, NH])).then_inc(S["cst_in"], 16)
            load_unit(Idx(2), in_cols(GATE_COL0, Idx(1)))
            with sp.Fori(0, 2) as i:
                for p in range(2):
                    for j in range(3):
                        load_unit(Idx(U_GDN_A + 3 * p + j, 6, i), in_cols(GDN_COL0 + j * NH * HD, Idx(p, 2, i)))
            load_unit(Idx(U_GATE_B), in_cols(GATE_COL0, Idx(2)))
            sp.wait_ge(S["fab_stored"], 4 * 16)
            for g in range(2):
                last = (U_GDN_A + 12 if g == 0 else U_STEP0 + 12) - 2
                for f in (last, last - 1):
                    sp.wait_ge(stored[f % 2], 16 * (f // 2 + 1))
                for i in range(2):
                    for p in range(2):
                        n, c = Idx(4 * g + p, 2, i), Idx(p, 2, i)
                        tok = bass.ds((c * CK).v, CK)
                        wait(S["step_free"], n + 1)
                        for part in range(3):
                            sp.dma_start(heads(kqv[p][:, part * 512:(part + 1) * 512]),
                                         qkv_d[0, GRP * g:GRP * g + GRP, part, :, tok].rearrange("h d t -> d h t"))\
                              .then_inc(step_in[p], 16)
                        sp.dma_start(heads(gcb[p][:, :]),
                                     rows_d[NH + GRP * g:NH + GRP * g + GRP, tok].unsqueeze(0)
                                     .to_broadcast([P, GRP, CK])).then_inc(step_in[p], 16)
                        sp.dma_start(sct[p][:, :], sct_d[g, bass.ds(c.v, 1), :, :].rearrange("a p c -> (a p) c"))\
                          .then_inc(step_in[p], 16)
                        u = Idx((U_STEP1 if g else U_STEP0) + 3 * p, 6, i)
                        for j in range(3):
                            if g == 0:
                                load_unit(u + j, in_cols(GDN_COL0 + j * NH * HD, c + GRP))
                            else:
                                load_unit(u + j, in_cols(j * NH * HD, c))
                            for k4 in ((0,), (1,), (2, 3))[j]:
                                load_ada(n + 8, k4, adw1)
                if g == 0:
                    load_unit(Idx(U_GATE_C), in_cols(GATE_COL0, Idx(3)))
            for second in range(2):
                for i in range(2):
                    for p in range(2):
                        m = Idx(4 * second + p, 2, i)
                        f = m * 3 + 30
                        for x in (f, f + -1):
                            wait(stored[x % 2], (x // 2 + 1) * 16)
                        wait(S["step_free"], m + 9)
                        sp.dma_start(kqv[p][:, :].rearrange("p (a t) -> p a t", a=3),
                                     qkv_d[1, bass.ds(m.v, 1), :, :, :].rearrange("m a d t -> d (m a) t"))\
                          .then_inc(step_in[p], 16)
                        sp.dma_start(gcb[p][:, :], rows_d[bass.ds(m.v, 1), :].to_broadcast([P, T]))\
                          .then_inc(step_in[p], 16)
                        if not second:
                            for j in range(3):
                                load_unit(Idx(U_FOXA + 3 * p + j, 6, i), in_cols(j * NH * HD, m + GRP))
                                for k4 in ((0,), (1,), (2, 3))[j]:
                                    load_ada(m + 16, k4, adw1)
                        else:
                            if m.base == GRP:
                                load_unit(Idx(U_FOXB), in_cols(GATE_COL0, m))
                            if m.base < NH - 1:
                                load_unit(Idx(U_FOXB + 1 + p, 2, i), in_cols(GATE_COL0, m + 1))
                            else:
                                load_unit(Idx(U_OUT), w_out[:, 0:P])
                            for k4 in range(4):
                                load_ada(m + 16, k4, adw1)

            def out_loads(k):
                if k.base >= 2:
                    wait(S["xb_t"], k + -1)
                cols = bass.ds((k * P).v, P)
                sp.dma_start(x_blk[k % 2][:, :].rearrange("p (b c) -> p b c", b=4),
                             I["x"][0, :, cols].rearrange("(b p) c -> p b c", p=P)).then_inc(xb_in[k % 2], 16)

            def out_unit(k):
                load_unit(k + U_OUT, w_out[:, bass.ds((k * P).v, P)])

            out_unit(Idx(1))
            sp.wait_ge(S["y_stored"], 16 * 16)
            for r in range(2):
                sp.wait_ge(stored[r], 16 * 28)
            sp.wait_ge(S["step_free"], 18)
            for kb in range(KB):
                if kb >= 2:
                    sp.wait_ge(S["y_split"], kb - 1)
                sp.dma_start(y_in[kb % 2][:, :], y_d[kb]).then_inc(yld[kb % 2], 16)
                if kb >= NH:
                    sp.dma_start(g_in[kb % 2][:, :], gate_d[kb - NH]).then_inc(gld[kb % 2], 16)
            out_loads(Idx(0))
            out_loads(Idx(1))
            with sp.Fori(0, KB // 2 - 1) as i:
                for p in range(2):
                    out_loads(Idx(2 + p, 2, i))
                    out_unit(Idx(2 + p, 2, i))

            def ffn_loads(i, it):
                for j in range(GRP):
                    for half in range(2):
                        load_unit(Idx(U_FFN + 2 * j + half, 12, i) if i is not None else Idx(U_FFN + 12 * it + 2 * j + half),
                                  w_up[:, bass.ds(((Idx(j, GRP, i) if i is not None else Idx(GRP * it + j)) * P
                                                   + half * FF).v, P)])
                for q in range(4):
                    row = Idx(0, 512, i) if i is not None else Idx(512 * it)
                    load_unit(Idx(U_FFN + 8 + q, 12, i) if i is not None else Idx(U_FFN + 12 * it + 8 + q),
                              w_down[bass.ds(row.v, 512), q * 512:(q + 1) * 512], blocks=4)

            with sp.Fori(0, FB // GRP - 1) as i:
                ffn_loads(i, 0)
            ffn_loads(None, FB // GRP - 1)
            for k in range(KB):
                sp.wait_ge(S["out_evac"], k + 1)
                sp.dma_start(out[0, :, k * P:(k + 1) * P].rearrange("(b p) c -> p b c", p=P),
                             o_tok[k % 2][:, :].rearrange("p (b c) -> p b c", b=4)).then_inc(out_stored[k % 2], 16)
            for r in range(2):
                sp.wait_ge(out_stored[r], 16 * KB // 2)

        @block.tensor
        def _(pe):
            mm = nc.tensor.matmul

            def unit_matmuls(u, a, first=None):
                if a.base >= 2:
                    pe.wait_ge(S["acc_evac"], (a + -1).v)
                for half in range(2):
                    piece = u * 2 + half
                    pe.wait_ge(S["lo_ready"], (piece + 1).v)
                    hi, lo = piece_at(w_hi, piece), piece_at(w_lo, piece)
                    for kk in range(8):
                        k = 8 * half + kk
                        if first:
                            pe.wait_ge(S[first], k + 1)
                        c = slice(kk * P, (kk + 1) * P)
                        mm(acc[u % 2][:, :], hi[:, c], xs(x_hi, k), start=k == 0, stop=False)
                        yield
                        mm(acc[u % 2][:, :], hi[:, c], xs(x_lo, k), start=False, stop=False)
                        yield
                        last = mm(acc[u % 2][:, :], lo[:, c], xs(x_hi, k), start=False, stop=k == KB - 1)
                        if kk == 7:
                            last.then_inc(S["piece_used"], 1)
                        yield

            def run(stream, n):
                for _ in range(n):
                    next(stream)

            def per_head(out_, lhs, rhs):
                for h in range(GRP):
                    c = slice(h * P, (h + 1) * P)
                    last = mm(out_[:, c], lhs[:, c], rhs[:, c], start=True, stop=True)
                return last

            def turn(out_, in_):
                for h in range(GRP):
                    c = slice(h * P, (h + 1) * P)
                    last = nc.tensor.transpose(out_[:, c], in_[:, c], ident)
                return last

            def ada_sum(sl, tile):
                pe.wait_ge(S["ada_acc_ready"], (sl + 1).v)
                for c in range(4):
                    last = mm(nb[:, c:c + 1], tile[:, c * P:(c + 1) * P], ones[:, 0:1], start=True, stop=True)
                last.then_inc(S["ada_sum_done"], 1)

            def sum_squares(cc):
                pe.wait_ge(S["sq_ready"], (cc + 1).v)
                mm(nb[:, :], ones, sq_t[:, :], start=True, stop=True).then_inc(S["ssq_done"], 1)

            pe.wait_ge(S["const_in"], 32)
            pe.wait_ge(S["vecrows_in"], 13 * 16)
            for r in range(6):
                last = nc.tensor.transpose(G[r // 4][:, (r % 4) * P:(r % 4 + 1) * P], rows_in[:, r * P:(r + 1) * P], ident)
            last.then_inc(S["vec_t"], 1)
            for b in range(4):
                pe.wait_ge(S["x_scaled"], b + 1)
                for k4 in range(4):
                    idx = 4 * b + k4
                    if idx >= 2:
                        pe.wait_ge(S["xn_ready"], idx - 1)
                    for j in range(4):
                        k = 4 * k4 + j
                        last = nc.tensor.transpose(G[2 + idx % 2][:, j * P:(j + 1) * P],
                                                   x_tok[:, (b % 2) * D + k * P:(b % 2) * D + (k + 1) * P], ident)
                    last.then_inc(S["xt_done"], 1)
            with pe.Fori(0, 8) as i:
                ada_sum(Idx(0, 1, i), ada_acc0)
            run(unit_matmuls(Idx(U_FAB), Idx(U_FAB), first="h_ready"), 48)
            st = unit_matmuls(Idx(1), Idx(1))
            run(st, 12)
            pe.wait_ge(S["acc_evac"], 1)
            turn(G[0], at_t).then_inc(S["fab_t"], 1)
            run(st, 36)
            st = unit_matmuls(Idx(2), Idx(2))
            run(st, 24)
            pe.wait_ge(S["fab_lg"], 1)
            mm(G[1][:, 0:64], cs(C_INC), so_t[:, 0:64], start=True, stop=True)
            mm(G[1][:, 64:128], ones, so_t[:, 0:64], start=True, stop=True).then_inc(S["fab_cum"], 1)
            run(st, 24)
            pe.wait_ge(S["fab_dve"], 2)
            for c in range(NCK):
                last = nc.tensor.transpose(G[2][0:2 * NH, c * P:(c + 1) * P], so_t[:, 128 + c * 16:144 + c * 16], ident)
            last.then_inc(S["rows_t"], 1)
            with pe.Fori(0, 2) as i:
                for p in range(2):
                    hh = Idx(p, 2, i)
                    for j in range(3):
                        st = unit_matmuls(Idx(U_GDN_A + 3 * p + j, 6, i), Idx(U_GDN_A + 3 * p + j, 6, i))
                        run(st, 24)
                        if j:
                            sum_squares(hh * 2 + (j - 1))
                        run(st, 24)
            run(unit_matmuls(Idx(U_GATE_B), Idx(U_GATE_B)), 48)

            def step(n, g, p, u, norms):
                kp, qp = kqv[p][:, 512:1024], kqv[p][:, 0:512]
                pe.wait_ge(step_in[p], ((n // 2 + 1) * 80).v)
                pe.wait_ge(S["state_ready"], (n + 1 + g).v)
                st = unit_matmuls(u, u)
                per_head(G[0], kp, kp)
                per_head(G[1], kp, qp).then_inc(S["scores_done"], 1)
                run(st, 6)
                pe.wait_ge(S["ot_evac"], (n + 1).v)
                turn(G[2], kp)
                turn(G[3], kqv[p][:, 1024:1536]).then_inc(S["tok_done"], 1)
                run(st, 6)
                per_head(G[4], kp, S_t).then_inc(S["ks_done"], 1)
                pe.wait_ge(S["up_ready"], (n + 1).v)
                turn(G[0], Up_t).then_inc(S["lt_done"], 1)
                run(st, 6)
                pe.wait_ge(S["attn_ready"], (n + 1).v)
                per_head(G[1], qp, S_t).then_inc(S["qs_done"], 1)
                run(st, 6)
                for slot in range(1, 4):
                    if slot == 2:
                        st = unit_matmuls(u + 1, u + 1)
                        if norms is not None:
                            sum_squares(norms)
                    for l in (2 * slot - 2, 2 * slot - 1):
                        if l == 0:
                            pe.wait_ge(S["tok_evac"], (n + 1).v)
                        pe.wait_ge(S["x_ready"], (n * NL + l + 1).v)
                        pe.wait_ge(S["upb_ready"], (n * NL + l + 1).v)
                        per_head(G[2], Upb[l % 2], X_t).then_inc(S["y_done"], 1)
                        run(st, 6)
                        pe.wait_ge(S["ys_ready"], (n * NL + l + 1).v)
                        if l < NL - 1:
                            per_head(G[4], XT_t, Ys_t)
                        per_head(G[3], Ys_t, XT_t).then_inc(S["z_done"], 1)
                        run(st, 6)
                st = unit_matmuls(u + 2, u + 2)
                if norms is not None:
                    sum_squares(norms + 1)
                pe.wait_ge(S["xt_final"], (n + 1).v)
                per_head(G[0], XT_t, R_t).then_inc(S["xr_done"], 1)
                run(st, 8)
                pe.wait_ge(S["vn_ready"], (n + 1).v)
                per_head(G[1], at_t, vn_t).then_inc(S["av_done"], 1)
                run(st, 6)
                pe.wait_ge(S["vnt_ready"], (n + 1).v)
                per_head(G[2], kt_t, vnt_t).then_inc(S["kv_done"], 1)
                run(st, 22)
                pe.wait_ge(S["on_ready"], (n + 1).v)
                turn(G[3], o_t).then_inc(S["ot_done"], 1)
                run(st, 6)
                ada_sum(n + 8, ada_acc1)
                run(st, 6)

            for g in range(2):
                with pe.Fori(0, 2) as i:
                    for p in range(2):
                        n = Idx(4 * g + p, 2, i)
                        step(n, g, p, Idx((U_STEP1 if g else U_STEP0) + 3 * p, 6, i),
                             None if g else (n + GRP) * 2)
                if g == 0:
                    run(unit_matmuls(Idx(U_GATE_C), Idx(U_GATE_C)), 48)

            def attend(m, p, streams):
                n = m + 8
                gaps = {3: (6, 42, 48, 48), 1: (6, 14, 14, 14)}[len(streams)]

                def gen():
                    for s in streams:
                        yield from unit_matmuls(s, s)
                st = gen()
                q, k, v = (kqv[p][:, a * 512:(a + 1) * 512] for a in range(3))
                pe.wait_ge(step_in[p], ((m // 2 + 1) * 32 + 320).v)
                pe.wait_ge(S["step_free"], (n + 2).v)
                pe.wait_ge(S["ot_evac"], (n + 1).v)
                turn(G[0], v).then_inc(S["fox_v_done"], 1)
                for b in range(4):
                    w_ = (b + 1) * P
                    mm(G[1 + b][:, 0:w_], q[:, b * P:(b + 1) * P], k[:, 0:w_], start=True, stop=True)\
                        .then_inc(S["fox_s_done"], 1)
                    if b % 2:
                        run(st, gaps[0])
                for b in range(4):
                    pe.wait_ge(S["fox_p_ready"], (m * 4 + b + 1).v)
                    for j in range(b + 1):
                        last = nc.tensor.transpose(G[1 + b][:, j * P:(j + 1) * P],
                                                   P_t[:, POFF[b] + j * P:POFF[b] + (j + 1) * P], ident)
                    last.then_inc(S["fox_pt_done"], 1)
                run(st, gaps[1])
                pe.wait_ge(S["fox_vt_ready"], (m + 1).v)
                pe.wait_ge(S["fox_pt_ready"], (m * 4 + 4).v)
                for b in range(4):
                    for j in range(b + 1):
                        last = mm(G[0][:, b * P:(b + 1) * P], PT_t[:, POFF[b] + j * P:POFF[b] + (j + 1) * P],
                                  vtok_t[:, j * P:(j + 1) * P], start=j == 0, stop=j == b)
                last.then_inc(S["fox_pv_done"], 1)
                run(st, gaps[2])
                pe.wait_ge(S["on_ready"], (n + 1).v)
                turn(G[1], o_t).then_inc(S["ot_done"], 1)
                run(st, len(streams) * 48 - 2 * gaps[0] - gaps[1] - gaps[2])
                ada_sum(m + 16, ada_acc1)

            for second in range(2):
                with pe.Fori(0, 2) as i:
                    for p in range(2):
                        m = Idx(4 * second + p, 2, i)
                        us = [Idx(U_FOXB + p, 2, i)] if second else [Idx(U_FOXA + 3 * p + j, 6, i) for j in range(3)]
                        attend(m, p, us)

            pe.wait_ge(S["y_split"], KB)
            with pe.Fori(0, 8) as i:
                for p in range(2):
                    k = Idx(p, 2, i)
                    pe.wait_ge(xb_in[p], ((k // 2 + 1) * 16).v)
                    turn(G[p], x_blk[p]).then_inc(S["xb_t"], 1)
                    run(unit_matmuls(k + U_OUT, k + U_OUT), 48)
            pe.wait_ge(S["ssum_ready"], KB + 1)
            mm(nb[:, :], ones, g_t[:, :], start=True, stop=True).then_inc(S["nsum_done"], 1)
            for k in range(KB):
                pe.wait_ge(S["xsq_ready"], k + 1)
                mm(G[0][:, :], ones, sqs[k % 2][:, :], start=k == 0, stop=k == KB - 1).then_inc(S["nsum2_done"], 1)

            pe.wait_ge(S["h2_ready"], KB)

            def ffn(at):
                for j in range(8):
                    run(unit_matmuls(at(U_FFN + j, 12), at(U_FFN + j, 8)), 48)
                for q in range(4):
                    for half in range(2):
                        piece = at(2 * (U_FFN + 8 + q) + half, 24)
                        pe.wait_ge(S["lo_ready"], (piece + 1).v)
                        hi, lo = piece_at(w_hi, piece), piece_at(w_lo, piece)
                        for kk in (2 * half, 2 * half + 1):
                            if q == 0:
                                pe.wait_ge(S["hidden_ready"], at(kk + 1, 4).v)
                            for dt in range(4):
                                if kk == 0 and q:
                                    pe.wait_ge(S["acc_added"], at(4 * q + dt - 3, 16).v)
                                c = slice((kk % 2) * 512 + dt * P, (kk % 2) * 512 + (dt + 1) * P)
                                mm(G[dt][:, :], hi[:, c], xs(hid_hi, kk), start=kk == 0, stop=False)
                                mm(G[dt][:, :], hi[:, c], xs(hid_lo, kk), start=False, stop=False)
                                last = mm(G[dt][:, :], lo[:, c], xs(hid_hi, kk), start=False, stop=kk == 3)
                                if kk % 2 == 1 and dt == 3:
                                    last.then_inc(S["piece_used"], 1)
                                elif kk == 3:
                                    last.then_inc(S["down_done"], 1)

            with pe.Fori(0, FB // GRP - 1) as i:
                ffn(lambda b, s: Idx(b, s, i))
            ffn(lambda b, s: Idx(b + s * (FB // GRP - 1)))
            for k in range(KB):
                pe.wait_ge(S["osq_ready"], k + 1)
                mm(nb[:, :], ones, osq[k % 2], start=k == 0, stop=k == KB - 1).then_inc(S["nsum3_done"], 1)
            for k in range(KB):
                pe.wait_ge(S["fin_x"], k + 1)
                if k >= 2:
                    pe.wait_ge(S["out_evac"], k - 1)
                turn(G[k % 2], xs(accT, k)).then_inc(S["out_t"], 1)

        @block.scalar
        def _(act):
            A = nc.scalar.activation
            ch = Chain(act, S["act_chain"])

            def prep(piece, last=False):
                if last:
                    return
                u = piece // 2 if piece.stride % 2 == 0 else None
                if piece.base < 2:
                    act.wait_ge(S["fab_in"], 32)
                else:
                    act.wait_ge(raw_landed[u % 2], landed(u).v)
                if piece.base >= 4:
                    act.wait_ge(S["piece_used"], (piece + -3).v)
                src = raw[:, (u % 2) * 2048 + (piece % 2) * 1024:(u % 2) * 2048 + (piece % 2 + 1) * 1024]
                A(piece_at(w_hi, piece), src, ACT.Copy).then_inc(S["hi_ready"], 1)

            def store_fin(f, dst):
                act.dma_start(dst, fin[f % 2][:, :]).then_inc(stored[f % 2], 16)

            def fin_free(f):
                if f.base >= 2:
                    act.wait_ge(stored[f % 2], stores_before(f).v)

            def qkv_at(kind, head, part):
                return qkv_d[kind, bass.ds(head.v, 1), part, :, :].rearrange("h d t -> (h d) t")

            def post_plain(u, func, dst):
                f = u + -1
                act.wait_ge(S["piece_used"], (u * 2 + 2).v)
                fin_free(f)
                A(fin[f % 2][:, :], acc[u % 2][:, :], func).then_inc(S["acc_evac"], 1)
                act.wait_ge(S["acc_evac"], (u + 1).v)
                store_fin(f, dst)

            def gate_at(head):
                return gate_d[bass.ds(head.v, 1), :, :].rearrange("h d t -> (h d) t")

            def post_gdn(u, hh, j):
                act.wait_ge(S["piece_used"], (u * 2 + 2).v)
                A(pre[:, 3:], acc[u % 2][:, :], ACT.Copy).then_inc(S["acc_evac"], 1)
                act.wait_ge(S["conv_ready"], (hh * 3 + j + 1).v)
                if j < 2:
                    ch(A(act_t[:, :], act_t[:, :], ACT.Silu))
                    A(sq_t[:, :], act_t[:, :], ACT.Square).then_inc(S["sq_ready"], 1)
                else:
                    f = u + -1
                    fin_free(f)
                    ch(A(fin[f % 2][:, :], act_t[:, :], ACT.Silu))
                    store_fin(f, qkv_at(0, hh, 2))

            def norm_gdn(hh, j):
                cc = hh * 2 + j
                act.wait_ge(S["ssq_done"], (cc + 1).v)
                ch(A(sq_t[:, :], nb[:, :], ACT.Ln, bias=eps[:, 0:1]))
                A(sq_t[:, :], sq_t[:, :], ACT.Exp, scale=-0.5).then_inc(S["rs_ready"], 1)

            def store_normed(u, hh, j):
                act.wait_ge(S["mul_ready"], (hh * 2 + j + 1).v)
                store_fin(u + -1, qkv_at(0, hh, j))

            act.wait_ge(S["cleared"], 2)
            A(rstd0[:, 4:5], rstd0[:, 5:6], ACT.Copy).then_inc(S["ot_evac"], 1)
            act.wait_ge(S["const_in"], 32)
            for b in range(4):
                xb = x_tok[:, (b % 2) * D:(b % 2 + 1) * D]
                if b >= 2:
                    act.wait_ge(S["xt_done"], 4 * (b - 1))
                    act.dma_start(xb, I["x"][0, b * P:(b + 1) * P, :]).then_inc(S["x_in"], 16)
                act.wait_ge(S["x_in"], 16 * (b + 1))
                ch(A(junk0[:, :], xb, ACT.Square, accum_out=rstd0[:, b:b + 1]))
                ch(A(rstd0[:, b:b + 1], rstd0[:, b:b + 1], ACT.Ln, scale=1.0 / D, bias=eps[:, 0:1]))
                ch(A(rstd0[:, b:b + 1], rstd0[:, b:b + 1], ACT.Exp, scale=-0.5))
                A(xb, xb, ACT.Copy, scale=rstd0[:, b:b + 1]).then_inc(S["x_scaled"], 1)
                if b == 0:
                    act.wait_ge(S["vec_ready"], 1)
                    A(cond[:, :], vec[:, V_C:V_C + KB], ACT.Silu).then_inc(S["cond_ready"], 1)
                for k4 in range(4):
                    idx = 4 * b + k4
                    act.wait_ge(S["xt_done"], idx + 1)
                    A(xnT[:, :].rearrange("p (k t) -> p k t", k=KB)[:, 4 * k4:4 * k4 + 4, b * P:(b + 1) * P],
                      G[2 + idx % 2][:, :].rearrange("p (k t) -> p k t", k=4), ACT.Copy).then_inc(S["xn_ready"], 1)
            for pc in range(2):
                prep(Idx(pc))
            for k in range(KB):
                act.wait_ge(S["h_tmp"], k + 1)
                A(xs(x_hi, k), xs(xnT, k), ACT.Copy).then_inc(S["h_hi_done"], 1)
            prep(Idx(2))
            prep(Idx(3))
            act.wait_ge(S["piece_used"], 2)
            A(at_t, acc[0][:, :], ACT.Copy).then_inc(S["acc_evac"], 1)
            prep(Idx(4))
            act.wait_ge(S["fab_t"], 1)
            A(ta_t, G[0][:, :], ACT.Copy).then_inc(S["fab_k"], 1)
            act.wait_ge(S["cst_in"], 64)
            ch(A(hb[:, 24:32], hb[:, 16:24], ACT.Exp))
            act.wait_ge(S["fab_dve"], 1)
            ch(A(D_t[:, 128:192], D_t[:, 64:128], ACT.Exp, scale=-1.0))
            ch(A(D_t[:, 192:256], D_t[:, 128:192], ACT.Ln, bias=eps[:, 1:2]))
            A(D_t[:, 256:288].rearrange("p (c h) -> p c h", c=NCK),
              heads(ta_t)[:, :, 16:24], ACT.Exp, scale=-1.0).then_inc(S["fab_act"], 1)
            prep(Idx(5))
            post_plain(Idx(1), ACT.Silu, gate_at(Idx(0)))
            prep(Idx(6))
            act.wait_ge(S["fab_dve"], 2)
            A(Up_t[:, 0:96], D_t[:, 320:416], ACT.Exp).then_inc(S["fab_act"], 1)
            act.wait_ge(S["fab_dve"], 3)
            for g in range(2):
                act.dma_start(sct_d[g].rearrange("c p s -> p c s"),
                              BM_t[:, 80 * g:80 * g + 80].rearrange("p (c s) -> p c s", c=NCK)).then_inc(S["fab_stored"], 16)
            prep(Idx(7))
            post_plain(Idx(2), ACT.Silu, gate_at(Idx(1)))
            act.wait_ge(S["rows_t"], 1)
            ch(A(X_t[0:2 * NH, :], G[2][0:2 * NH, :], ACT.Copy))
            act.dma_start(rows_d[0:NH, :], X_t[0:NH, :]).then_inc(S["fab_stored"], 16)
            act.dma_start(rows_d[NH:2 * NH, :], X_t[NH:2 * NH, :]).then_inc(S["fab_stored"], 16)
            ch.loop(None, 0)
            ch.end(1)
            with act.Fori(0, 2) as i:
                ch.loop(i, 10)
                for p in range(2):
                    hh = Idx(p, 2, i)
                    for j in range(3):
                        u = Idx(U_GDN_A + 3 * p + j, 6, i)
                        prep(u * 2 + 2)
                        if j:
                            norm_gdn(hh, j - 1)
                            store_normed(u + -1, hh, j - 1)
                        prep(u * 2 + 3)
                        post_gdn(u, hh, j)
                    pass
                ch.end(2)
            prep(Idx(2 * U_GATE_B + 2))
            prep(Idx(2 * U_GATE_B + 3))
            post_plain(Idx(U_GATE_B), ACT.Silu, gate_at(Idx(2)))

            def norm_o(n):
                act.wait_ge(S["oss_ready"], (n + 1).v)
                ch(A(st1[:, 4:8], st1[:, 0:4], ACT.Ln, scale=1.0 / HD, bias=eps[:, 0:1]))
                A(st1[:, 4:8], st1[:, 4:8], ACT.Exp, scale=-0.5).then_inc(S["orr_ready"], 1)

            def out_head(n, bank, gain, dst):
                act.wait_ge(S["ot_done"], (n + 1).v)
                A(oT[:, :], bank[:, :], ACT.Copy, scale=vec[:, gain:gain + 1]).then_inc(S["ot_evac"], 1)
                act.wait_ge(S["ot_evac"], (n + 2).v)
                act.dma_start(dst[0], dst[1]).then_inc(S["y_stored"], 16)

            def step(n, g, p, c, u, hh):
                prep(u * 2 + 2)
                act.wait_ge(S["dif_ready"], (n + 1).v)
                A(D_t, D_t, ACT.Exp).then_inc(S["d_ready"], 1)
                act.wait_ge(S["tok_done"], (n + 1).v)
                A(kt_t, G[2][:, :], ACT.Copy)
                A(R_t, G[3][:, :], ACT.Copy).then_inc(S["tok_evac"], 1)
                for slot in range(1, 4):
                    prep(u * 2 + slot + 2)
                    for l in (2 * slot - 2, 2 * slot - 1):
                        act.wait_ge(S["y_done"], (n * NL + l + 1).v)
                        A(Ys_t, G[2][:, :], ACT.Copy).then_inc(S["ys_ready"], 1)
                        if slot == 2 and l == 2 and hh is not None:
                            norm_gdn(hh, 0)
                    if slot == 2 and hh is not None:
                        store_normed(u, hh, 0)
                    if slot in (1, 3):
                        post(u, hh, c, slot // 2)
                prep(u * 2 + 6)
                if hh is not None:
                    norm_gdn(hh, 1)
                    store_normed(u + 1, hh, 1)
                norm_o(n)
                prep(u * 2 + 7)
                out_head(n, G[3], V_GDNN, (y_d[NH + GRP * g:NH + GRP * g + GRP, :, bass.ds((c * CK).v, CK)]
                                           .rearrange("h d t -> d h t"), heads(oT[:, :])))
                post(u, hh, c, 2)
                act.wait_ge(S["y_stored"], ((n + 1) * 16).v)

            def post(u, hh, c, j):
                if hh is not None:
                    post_gdn(u + j, hh, j)
                else:
                    post_plain(u + j, ACT.Copy, qkv_at(1, c, j))

            for g in range(2):
                with act.Fori(0, 2) as i:
                    ch.loop(i, 2 * (6 if g == 0 else 1))
                    for p in range(2):
                        n, c = Idx(4 * g + p, 2, i), Idx(p, 2, i)
                        step(n, g, p, c, Idx((U_STEP1 if g else U_STEP0) + 3 * p, 6, i), None if g else c + GRP)
                    ch.end(2)
                if g == 0:
                    prep(Idx(2 * U_GATE_C + 2))
                    prep(Idx(2 * U_GATE_C + 3))
                    post_plain(Idx(U_GATE_C), ACT.Silu, gate_at(Idx(3)))

            def attend(m, p, second, us):
                n = m + 8
                prep(us[0] * 2 + 2)
                act.wait_ge(S["fox_v_done"], (m + 1).v)
                A(vtok_t, G[0][:, :], ACT.Copy).then_inc(S["fox_vt_ready"], 1)
                for b in range(4):
                    act.wait_ge(S["fox_m_ready"], (m * 4 + b + 1).v)
                    row = P_t[:, POFF[b]:POFF[b] + (b + 1) * P]
                    A(row, row, ACT.Exp, bias=st1[:, 8 + b:9 + b], accum_out=st1[:, 12 + b:13 + b])\
                        .then_inc(S["fox_p_ready"], 1)
                for b in range(4):
                    act.wait_ge(S["fox_pt_done"], (m * 4 + b + 1).v)
                    w_ = (b + 1) * P
                    A(PT_t[:, POFF[b]:POFF[b] + w_], G[1 + b][:, 0:w_], ACT.Copy).then_inc(S["fox_pt_ready"], 1)
                prep(us[0] * 2 + 3)
                if not second:
                    post(us[0], None, m + GRP, 0)
                    prep(us[0] * 2 + 4)
                norm_o(n)
                if not second:
                    prep(us[0] * 2 + 5)
                    post(us[0], None, m + GRP, 1)
                    prep(us[0] * 2 + 6)
                out_head(n, G[1], V_FOXN, (y_d[bass.ds(m.v, 1), :, :].rearrange("m d t -> (m d) t"), oT[:, :]))
                if not second:
                    prep(us[0] * 2 + 7)
                    post(us[0], None, m + GRP, 2)
                else:
                    post_plain(us[0], ACT.Silu, gate_at(m))
                act.wait_ge(S["y_stored"], ((n + 1) * 16).v)

            for second in range(2):
                with act.Fori(0, 2) as i:
                    ch.loop(i, 2)
                    for p in range(2):
                        m = Idx(4 * second + p, 2, i)
                        us = [Idx(U_FOXB + p, 2, i)] if second else [Idx(U_FOXA + 3 * p, 6, i)]
                        attend(m, p, second, us)
                    ch.end(2)
            for kb in range(KB):
                if kb < NH:
                    act.wait_ge(yld[kb % 2], 16 * (kb // 2 + 1))
                else:
                    act.wait_ge(S["y_mul"], kb - NH + 1)
                if kb == 0:
                    act.wait_ge(S["piece_used"], 2 * U_OUT)
                A(xs(x_hi, kb), y_in[kb % 2][:, :], ACT.Copy).then_inc(S["y_hi"], 1)
            with act.Fori(0, 8) as i:
                for p in range(2):
                    k = Idx(p, 2, i)
                    u = k + U_OUT
                    prep(u * 2 + 2)
                    prep(u * 2 + 3)
                    act.wait_ge(S["piece_used"], (u * 2 + 2).v)
                    act.wait_ge(S["ssum_ready"], (k + 1).v)
                    A(sqs[0][:, :], acc[u % 2][:, :], ACT.Square).then_inc(S["sq_out"], 1)
                    A(accT[:, bass.ds((k * T).v, T)], acc[u % 2][:, :], ACT.Copy).then_inc(S["acc_evac"], 1)
            act.wait_ge(S["nsum_done"], 1)
            ch(A(v_t[:, :], nb[:, :], ACT.Ln, scale=1.0 / D, bias=eps[:, 0:1]))
            A(v_t[:, :], v_t[:, :], ACT.Exp, scale=-0.5).then_inc(S["r_ready"], 1)
            for k in range(KB):
                act.wait_ge(S["x1_ready"], k + 1)
                if k >= 2:
                    act.wait_ge(S["nsum2_done"], k - 1)
                A(sqs[k % 2][:, :], xs(x1T, k), ACT.Square).then_inc(S["xsq_ready"], 1)
            act.wait_ge(S["nsum2_done"], KB)
            ch(A(g_t[:, :], G[0][:, :], ACT.Ln, scale=1.0 / D, bias=eps[:, 0:1]))
            A(g_t[:, :], g_t[:, :], ACT.Exp, scale=-0.5).then_inc(S["r2_ready"], 1)
            for k in range(KB):
                act.wait_ge(S["h2_tmp"], k + 1)
                A(xs(x_hi, k), xs(accT, k), ACT.Identity, bias=mod[:, 48 + k:49 + k]).then_inc(S["h2_hi"], 1)

            def ffn(at, final):
                for j in range(GRP):
                    for val in range(2):
                        jj = 2 * j + val
                        u = at(U_FFN + jj, 12)
                        prep(u * 2 + 2)
                        prep(u * 2 + 3)
                        act.wait_ge(S["piece_used"], (u * 2 + 2).v)
                        A(fpre[:, 2:], acc[u % 2][:, :], ACT.Copy).then_inc(S["acc_evac"], 1)
                        if not val:
                            act.wait_ge(S["fconv_ready"], at(j + 1, GRP).v)
                            A(g_t[:, :], g_t[:, :], ACT.Silu).then_inc(S["silu_ready"], 1)
                        else:
                            act.wait_ge(S["hidden_tmp"], at(j + 1, GRP).v)
                            A(xs(hid_hi, j), v_t[:, :], ACT.Copy).then_inc(S["hidden_hi"], 1)
                for q in range(4):
                    u = at(U_FFN + 8 + q, 12)
                    prep(u * 2 + 2, final and q == 3)
                    prep(u * 2 + 3, final and q == 3)

            with act.Fori(0, FB // GRP - 1) as i:
                ffn(lambda b, s: Idx(b, s, i), False)
            ffn(lambda b, s: Idx(b + s * (FB // GRP - 1)), True)
            for k in range(KB):
                act.wait_ge(S["acc_added"], FB // GRP * 16 - 15 + k)
                if k >= 2:
                    act.wait_ge(S["nsum3_done"], k - 1)
                A(osq[k % 2], xs(accT, k), ACT.Square).then_inc(S["osq_ready"], 1)
            act.wait_ge(S["nsum3_done"], KB)
            ch(A(v_t[:, :], nb[:, :], ACT.Ln, scale=1.0 / D, bias=eps[:, 0:1]))
            A(v_t[:, :], v_t[:, :], ACT.Exp, scale=-0.5).then_inc(S["r3_ready"], 1)
            for k in range(KB):
                act.wait_ge(S["out_t"], k + 1)
                if k >= 2:
                    act.wait_ge(out_stored[k % 2], 16 * (k // 2))
                A(o_tok[k % 2][:, :], G[k % 2][:, :], ACT.Copy).then_inc(S["out_evac"], 1)

        @block.gpsimd
        def _(pool):
            TT = nc.gpsimd.tensor_tensor

            def step(n, p):
                pool.wait_ge(step_in[p], ((n // 2 + 1) * 80).v)
                TT(heads(BM_t), mask(C_STR), over_free(sct[p][:, 4:8]), ALU.mult).then_inc(S["bm_ready"], 1)
                pool.wait_ge(S["up_ready"], (n + 1).v)
                for l in range(NL):
                    if l >= 2:
                        pool.wait_ge(S["y_done"], (n * NL + (l - 1)).v)
                    TT(heads(Upb[l % 2]), heads(Up_t), mask(C_MU + P * (l + 1)), ALU.mult).then_inc(S["upb_ready"], 1)
                    if l == 1:
                        pool.wait_ge(S["qs_done"], (n + 1).v)
                        TT(heads(S_t), heads(S_t), over_free(sct[p][:, 16:20]), ALU.mult).then_inc(S["s_decayed"], 1)
                pool.wait_ge(S["vn_ready"], (n + 1).v)
                TT(heads(vnt_t), heads(vn_t), over_free(sct[p][:, 12:16]), ALU.mult).then_inc(S["vnt_ready"], 1)
                squares(n)

            def squares(n):
                pool.wait_ge(S["o_ready"], (n + 1).v)
                TT(so_t, o_t, o_t, ALU.mult).then_inc(S["so_ready"], 1)

            pool.wait_ge(S["cst_in"], 64)
            for g in range(2):
                with pool.Fori(0, 2) as i:
                    for p in range(2):
                        step(Idx(4 * g + p, 2, i), p)
            with pool.Fori(0, 8) as i:
                squares(Idx(8, 1, i))
            pool.wait_ge(S["y_split"], KB)
            nc.gpsimd.memset(g_t[:, :], 0.0).then_inc(S["ssum_ready"], 1)
            with pool.Fori(0, KB) as i:
                k = Idx(0, 1, i)
                pool.wait_ge(S["sq_out"], (k + 1).v)
                pool.wait_ge(S["ssum_ready"], (k + 1).v)
                TT(g_t[:, :], g_t[:, :], sqs[0][:, :], ALU.add).then_inc(S["ssum_ready"], 1)
            pool.wait_ge(S["h2_ready"], KB)
            nc.gpsimd.memset(accT[:, :], 0.0).then_inc(S["acc_zero"], 1)

        @block.vector
        def _(v):
            TT, TS, STT = nc.vector.tensor_tensor, nc.vector.tensor_scalar, nc.vector.scalar_tensor_tensor
            ch = Chain(v, S["dve_chain"])

            def prep(piece, last=False):
                if last:
                    return
                u = piece // 2
                v.wait_ge(S["hi_ready"], (piece + 1).v)
                src = raw[:, (u % 2) * 2048 + (piece % 2) * 1024:(u % 2) * 2048 + (piece % 2 + 1) * 1024]
                TT(piece_at(w_lo, piece), src, piece_at(w_hi, piece).bitcast(F32), ALU.subtract).then_inc(S["lo_ready"], 1)

            def ada_add(sl, k4, tile, total):
                q = sl * 4 + k4
                v.wait_ge(ada_landed[q % 2], ((q // 2 + 1) * 16).v if q.stride % 2 == 0 else ((sl * 2 + k4 // 2 + 1) * 16).v)
                for kk in range(4):
                    k = 4 * k4 + kk
                    src = tile[:, (q % 2) * 2048 + kk * 512:(q % 2) * 2048 + (kk + 1) * 512]
                    if k == 0:
                        ch(TS(total[:, :], src, cond[:, 0:1], None, ALU.mult))
                    else:
                        ins = STT(total[:, :], src, cond[:, k:k + 1], total[:, :], ALU.mult, ALU.add)
                        if k == KB - 1:
                            ins.then_inc(S["ada_acc_ready"], 1)
                        elif kk == 3:
                            ins.then_inc(S["ada_used"], 1)
                            v.wait_ge(S["ada_used"], (q + 1).v)
                        else:
                            ch(ins)

            def ada_take(sl):
                v.wait_ge(S["ada_sum_done"], (sl + 1).v)
                nc.vector.tensor_copy(mod[:, bass.ds((sl * 4).v, 4)], nb[:, 0:4]).then_inc(S["ada_used"], 1)

            def conv_gdn(u, hh, j):
                v.wait_ge(S["acc_evac"], (u + 1).v)
                ch(TS(act_t[:, :], pre[:, 3:3 + T], cw[:, 4 * j + 3:4 * j + 4], None, ALU.mult))
                for tap in (2, 1):
                    ch(STT(act_t[:, :], pre[:, tap:tap + T], cw[:, 4 * j + tap:4 * j + tap + 1], act_t[:, :], ALU.mult, ALU.add))
                STT(act_t[:, :], pre[:, 0:T], cw[:, 4 * j:4 * j + 1], act_t[:, :], ALU.mult, ALU.add)\
                    .then_inc(S["conv_ready"], 1)
                if j == 2:
                    v.wait_ge(S["conv_ready"], (hh * 3 + 3).v)

            def normed(u, hh, j):
                f = u + -1
                v.wait_ge(S["rs_ready"], (hh * 2 + j + 1).v)
                if f.base >= 2:
                    v.wait_ge(stored[f % 2], stores_before(f).v)
                STT(fin[f % 2][:, :], act_t[:, :], 1.0 if j else QSCALE, sq_t[:, :], ALU.mult, ALU.mult)\
                    .then_inc(S["mul_ready"], 1)

            def conv_weights(hh):
                src = vec[:, V_GCONV:V_GCONV + 96].rearrange("p (t q h) -> p q t h", t=CONV, q=3)
                ch(nc.vector.tensor_copy(cw[:, :].rearrange("p (q t) -> p q t", q=3).unsqueeze(3),
                                         src[:, :, :, bass.ds(hh.v, 1)]))

            nc.vector.memset(rows_in[:, :], 0.0).then_inc(S["cleared"], 1)
            ch(nc.vector.memset(rstd0[:, :], 0.0))
            nc.vector.memset(raw[:, 0:2048], 0.0).then_inc(S["cleared"], 1)
            v.wait_ge(S["vec_t"], 1)
            ch(nc.vector.tensor_copy(vec[:, 0:512], G[0][:, :]))
            nc.vector.tensor_copy(vec[:, 512:768], G[1][:, 0:256]).then_inc(S["vec_ready"], 1)
            v.wait_ge(S["vec_ready"], 1)
            v.wait_ge(S["cond_ready"], 1)
            with v.Fori(0, 8) as i:
                ch.loop(i, 12)
                for k4 in range(4):
                    ada_add(Idx(0, 1, i), k4, adw0, ada_acc0)
                ada_take(Idx(0, 1, i))
                ch.end(8)
            v.wait_ge(S["ada_used"], 32)
            ch(TT(mod[:, 0:32], mod[:, 0:32], vec[:, V_BADA:V_BADA + 32], ALU.add))
            ch(STT(s_mix[:, :], mod[:, 16:32], 1.0, vec[:, V_MIXPRE:V_MIXPRE + KB], ALU.add, ALU.mult))
            prep(Idx(0))
            prep(Idx(1))
            for k in range(KB):
                if k == 0:
                    v.wait_ge(S["xn_ready"], 16)
                TS(xs(xnT, k), xs(xnT, k), s_mix[:, k:k + 1], mod[:, k:k + 1], ALU.mult, ALU.add).then_inc(S["h_tmp"], 1)
                if k:
                    v.wait_ge(S["h_hi_done"], k)
                    TT(xs(x_lo, k - 1), xs(xnT, k - 1), xs(x_hi, k - 1).bitcast(F32), ALU.subtract).then_inc(S["h_ready"], 1)
            v.wait_ge(S["h_hi_done"], KB)
            TT(xs(x_lo, KB - 1), xs(xnT, KB - 1), xs(x_hi, KB - 1).bitcast(F32), ALU.subtract).then_inc(S["h_ready"], 1)
            prep(Idx(2))
            prep(Idx(3))
            v.wait_ge(S["h_ready"], KB)
            nc.vector.memset(st1[:, 20:21], 0.0).then_inc(S["step_free"], 1)
            nc.vector.memset(st1[:, 21:22], 0.0).then_inc(S["step_free"], 1)
            ch(nc.vector.memset(pre[:, 0:3], 0.0))
            prep(Idx(4))
            v.wait_ge(S["fab_k"], 1)
            v.wait_ge(S["cst_in"], 64)

            def q64(tile, at):
                return tile[:, at:at + 64].rearrange("p (c h) -> p c h", c=NCK)

            def q32(tile, at):
                return tile[:, at:at + 32].rearrange("p (c h) -> p c h", c=NCK)

            z, az, l = q64(D_t, 0), D_t[:, 64:128], q64(D_t, 192)
            ch(TT(z, heads(ta_t)[:, :, 0:16], hb[:, 0:16].unsqueeze(1).to_broadcast([P, NCK, 16]), ALU.add))
            ch(TS(az, D_t[:, 0:64], -1.0, None, ALU.mult))
            TT(az, az, D_t[:, 0:64], ALU.max).then_inc(S["fab_dve"], 1)
            v.wait_ge(S["fab_act"], 1)
            lg = q64(so_t, 0)
            ch(STT(lg[:, :, 0:8], z[:, :, 0:8], 0.0, l[:, :, 0:8], ALU.min, ALU.subtract))
            ch(STT(lg[:, :, 8:16], z[:, :, 8:16], 0.0, l[:, :, 8:16], ALU.max, ALU.add))
            ch(TS(hb[:, 24:32], hb[:, 24:32], -1.0, None, ALU.mult))
            TT(lg[:, :, 8:16], lg[:, :, 8:16], hb[:, 24:32].unsqueeze(1).to_broadcast([P, NCK, 8]), ALU.mult)\
                .then_inc(S["fab_lg"], 1)
            ch(TS(D_t[:, 256:288], D_t[:, 256:288], 1.0, None, ALU.add))
            ch(nc.vector.reciprocal(D_t[:, 288:320], D_t[:, 256:288]))
            prep(Idx(5))
            prep(Idx(6))
            v.wait_ge(S["fab_cum"], 1)
            ch(nc.vector.tensor_copy(at_t[:, 0:128], G[1][:, 0:128]))
            W_, Tt = q64(at_t, 0), q64(at_t, 64)
            rw = q64(so_t, 128)
            ch(nc.vector.tensor_copy(so_t[:, 128:192], at_t[:, 0:64]))
            for c in range(1, NCK):
                for c2 in range(c):
                    ch(TT(rw[:, c, 0:8], rw[:, c, 0:8], Tt[:, c2, 0:8], ALU.add))
            ch(nc.vector.tensor_copy(q32(D_t, 320), W_[:, :, 8:16]))
            ch(TT(q32(D_t, 352), Tt[:, :, 8:16], W_[:, :, 8:16], ALU.subtract))
            nc.vector.tensor_copy(q32(D_t, 384), Tt[:, :, 8:16]).then_inc(S["fab_dve"], 1)
            v.wait_ge(S["fab_act"], 2)
            for kind, tile, at in ((0, D_t, 320), (1, D_t, 288), (2, Up_t, 0), (3, Up_t, 32), (4, Up_t, 64)):
                for g in range(2):
                    dst = BM_t[:, 80 * g:80 * g + 80].rearrange("p (c s) -> p c s", c=NCK)[:, :, 4 * kind:4 * kind + 4]
                    ins = nc.vector.tensor_copy(dst, q32(tile, at)[:, :, 4 * g:4 * g + 4])
                    ch(ins) if (kind, g) != (4, 1) else ins.then_inc(S["fab_dve"], 1)
            prep(Idx(7))
            with v.Fori(0, 2) as i:
                ch.loop(i, 20)
                for p in range(2):
                    hh = Idx(p, 2, i)
                    conv_weights(hh)
                    for j in range(3):
                        u = Idx(U_GDN_A + 3 * p + j, 6, i)
                        prep(u * 2 + 2)
                        if j:
                            normed(u + -1, hh, j - 1)
                        prep(u * 2 + 3)
                        conv_gdn(u, hh, j)
                ch.end(2)
            prep(Idx(2 * U_GATE_B + 2))
            prep(Idx(2 * U_GATE_B + 3))

            def finish_o(n):
                v.wait_ge(S["so_ready"], (n + 1).v)
                nc.vector.reduce_sum(st1[:, 0:4], heads(so_t), AX.X).then_inc(S["oss_ready"], 1)

            def norm_o(n):
                v.wait_ge(S["orr_ready"], (n + 1).v)
                TT(heads(o_t), heads(o_t), over_free(st1[:, 4:8]), ALU.mult).then_inc(S["on_ready"], 1)
                v.wait_ge(S["step_free"], (n + 2).v)
                nc.vector.memset(st1[:, 20:21], 0.0).then_inc(S["step_free"], 1)

            def step(n, g, p, u, hh):
                gc, beta, egc = (over_free(sct[p][:, 4 * k:4 * k + 4]) for k in range(3))
                prep(u * 2 + 2)
                v.wait_ge(step_in[p], ((n // 2 + 1) * 80).v)
                ch(TT(heads(D_t), heads(gcb[p][:, :]), gc, ALU.subtract))
                TS(D_t, D_t, 0.0, None, ALU.min).then_inc(S["dif_ready"], 1)
                v.wait_ge(S["scores_done"], (n + 1).v)
                v.wait_ge(S["bm_ready"], (n + 1).v)
                ch(TT(ta_t, G[0][:, :], BM_t, ALU.mult))
                v.wait_ge(S["d_ready"], (n + 1).v)
                TT(Up_t, ta_t, D_t, ALU.mult).then_inc(S["up_ready"], 1)
                ch(TT(heads(at_t), heads(G[1][:, :]), mask(C_INC), ALU.mult))
                TT(at_t, at_t, D_t, ALU.mult).then_inc(S["attn_ready"], 1)
                v.wait_ge(S["up_ready"], (n + 1).v)
                ch(TT(heads(ta_t), heads(Up_t), mask(C_MU), ALU.mult))
                ch(TT(heads(XT_t), over_heads(ident), heads(ta_t), ALU.subtract))
                v.wait_ge(S["ks_done"], (n + 1).v)
                ch(TT(heads(ta_t), heads(G[4][:, :]), egc, ALU.mult))
                v.wait_ge(S["tok_evac"], (n + 1).v)
                ch(TT(R_t, R_t, ta_t, ALU.subtract))
                v.wait_ge(S["lt_done"], (n + 1).v)
                ch(TT(heads(ta_t), heads(G[0][:, :]), mask(C_ML1), ALU.mult))
                TT(heads(X_t), over_heads(ident), heads(ta_t), ALU.subtract).then_inc(S["x_ready"], 1)
                v.wait_ge(S["qs_done"], (n + 1).v)
                ch(TT(heads(o_t), heads(G[1][:, :]), egc, ALU.mult))
                if hh is not None:
                    conv_weights(hh)
                for slot in range(1, 4):
                    prep(u * 2 + slot + 2)
                    for l in (2 * slot - 2, 2 * slot - 1):
                        v.wait_ge(S["z_done"], (n * NL + l + 1).v)
                        v.wait_ge(S["x_ready"], (n * NL + l + 1).v)
                        ins = TT(XT_t, XT_t, G[3][:, :], ALU.subtract)
                        if l < NL - 1:
                            TT(X_t, X_t, G[4][:, :], ALU.subtract).then_inc(S["x_ready"], 1)
                        else:
                            ins.then_inc(S["xt_final"], 1)
                        if l == 2 and hh is not None:
                            normed(u, hh, 0)
                    ada_add(n + 8, slot - 1, adw1, ada_acc1)
                    if slot in (1, 3) and hh is not None:
                        conv_gdn(u + slot // 2, hh, slot // 2)
                prep(u * 2 + 6)
                v.wait_ge(S["xr_done"], (n + 1).v)
                TT(heads(vn_t), heads(G[0][:, :]), beta, ALU.mult).then_inc(S["vn_ready"], 1)
                if hh is not None:
                    normed(u + 1, hh, 1)
                v.wait_ge(S["av_done"], (n + 1).v)
                TT(o_t, o_t, G[1][:, :], ALU.add).then_inc(S["o_ready"], 1)
                v.wait_ge(S["kv_done"], (n + 1).v)
                v.wait_ge(S["s_decayed"], (n + 1).v)
                TT(S_t, S_t, G[2][:, :], ALU.add).then_inc(S["state_ready"], 1)
                finish_o(n)
                ada_add(n + 8, 3, adw1, ada_acc1)
                norm_o(n)
                prep(u * 2 + 7)
                ada_take(n + 8)
                if hh is not None:
                    conv_gdn(u + 2, hh, 2)

            for g in range(2):
                nc.vector.memset(S_t, 0.0).then_inc(S["state_ready"], 1)
                with v.Fori(0, 2) as i:
                    ch.loop(i, 2 * (9 + 12 + (10 if g == 0 else 0)))
                    for p in range(2):
                        n, c = Idx(4 * g + p, 2, i), Idx(p, 2, i)
                        step(n, g, p, Idx((U_STEP1 if g else U_STEP0) + 3 * p, 6, i), None if g else c + GRP)
                    ch.end(2)
                if g == 0:
                    prep(Idx(2 * U_GATE_C + 2))
                    prep(Idx(2 * U_GATE_C + 3))

            def attend(m, p, second, u):
                n = m + 8
                prep(u * 2 + 2)
                v.wait_ge(step_in[p], ((m // 2 + 1) * 32 + 320).v)
                for b in range(4):
                    w_ = (b + 1) * P
                    row = P_t[:, POFF[b]:POFF[b] + w_]
                    v.wait_ge(S["fox_s_done"], (m * 4 + b + 1).v)
                    ch(STT(row, G[1 + b][:, 0:w_], QSCALE, gcb[p][:, 0:w_], ALU.mult, ALU.subtract))
                    ch(TT(row[:, b * P:], row[:, b * P:], cs(C_NEG), ALU.add))
                    nc.vector.tensor_reduce(st1[:, 8 + b:9 + b], row, AX.X, ALU.max, negate=True)\
                        .then_inc(S["fox_m_ready"], 1)
                ada_add(m + 16, 0, adw1, ada_acc1)
                if second:
                    ada_add(m + 16, 1, adw1, ada_acc1)
                v.wait_ge(S["fox_p_ready"], (m * 4 + 4).v)
                ch(nc.vector.reciprocal(st1[:, 16:20], st1[:, 12:16]))
                prep(u * 2 + 3)
                if not second:
                    prep(u * 2 + 4)
                v.wait_ge(S["fox_pv_done"], (m + 1).v)
                TT(heads(o_t), heads(G[0][:, :]), over_free(st1[:, 16:20]), ALU.mult).then_inc(S["o_ready"], 1)
                finish_o(n)
                if not second:
                    ada_add(m + 16, 1, adw1, ada_acc1)
                norm_o(n)
                if not second:
                    prep(u * 2 + 5)
                ada_add(m + 16, 2, adw1, ada_acc1)
                if not second:
                    prep(u * 2 + 6)
                ada_add(m + 16, 3, adw1, ada_acc1)
                if not second:
                    prep(u * 2 + 7)
                ada_take(m + 16)

            for second in range(2):
                with v.Fori(0, 2) as i:
                    ch.loop(i, 2 * 21)
                    for p in range(2):
                        m = Idx(4 * second + p, 2, i)
                        attend(m, p, second, Idx(U_FOXB + p, 2, i) if second else Idx(U_FOXA + 3 * p, 6, i))
                    ch.end(2)
            v.wait_ge(S["ada_used"], 96)
            ch(TT(mod[:, 32:96], mod[:, 32:96], vec[:, V_BADA + 32:V_BADA + 96], ALU.add))
            ch(TT(g_mix[:, :], mod[:, 32:48], vec[:, V_MIXPOST:V_MIXPOST + KB], ALU.mult))
            ch(STT(s_ffn[:, :], mod[:, 64:80], 1.0, vec[:, V_FFNPRE:V_FFNPRE + KB], ALU.add, ALU.mult))
            ch(TT(g_ffn[:, :], mod[:, 80:96], vec[:, V_FFNPOST:V_FFNPOST + KB], ALU.mult))
            for kb in range(KB):
                v.wait_ge(yld[kb % 2], 16 * (kb // 2 + 1))
                if kb >= NH:
                    v.wait_ge(gld[kb % 2], 16 * ((kb - NH) // 2 + 1))
                    TT(y_in[kb % 2][:, :], y_in[kb % 2][:, :], g_in[kb % 2][:, :], ALU.mult).then_inc(S["y_mul"], 1)
                    v.wait_ge(S["y_mul"], kb - NH + 1)
                v.wait_ge(S["y_hi"], kb + 1)
                TT(xs(x_lo, kb), y_in[kb % 2][:, :], xs(x_hi, kb).bitcast(F32), ALU.subtract).then_inc(S["y_split"], 1)
            with v.Fori(0, 8) as i:
                for p in range(2):
                    k = Idx(p, 2, i)
                    u = k + U_OUT
                    prep(u * 2 + 2)
                    v.wait_ge(S["xb_t"], (k + 1).v)
                    nc.vector.tensor_copy(x1T[:, bass.ds((k * T).v, T)], G[p][:, :]).then_inc(S["xb_ready"], 1)
                    prep(u * 2 + 3)
            v.wait_ge(S["r_ready"], 1)
            v.wait_ge(S["xb_ready"], KB)
            for k in range(KB):
                ch(STT(xs(accT, k), xs(accT, k), g_mix[:, k:k + 1], v_t[:, :], ALU.mult, ALU.mult))
                TT(xs(x1T, k), xs(x1T, k), xs(accT, k), ALU.add).then_inc(S["x1_ready"], 1)
            v.wait_ge(S["r2_ready"], 1)
            for k in range(KB + 1):
                if k < KB:
                    STT(xs(accT, k), xs(x1T, k), s_ffn[:, k:k + 1], g_t[:, :], ALU.mult, ALU.mult).then_inc(S["h2_tmp"], 1)
                if k:
                    v.wait_ge(S["h2_hi"], k)
                    STT(xs(x_lo, k - 1), xs(accT, k - 1), mod[:, 47 + k:48 + k], xs(x_hi, k - 1).bitcast(F32),
                        ALU.add, ALU.subtract).then_inc(S["h2_ready"], 1)
            ch(nc.vector.memset(fpre[:, 0:2], 0.0))

            def ffn(at, final):
                taps = vec[:, V_FCONV:V_FCONV + 512].rearrange("p (r c) -> p r c", r=4)
                for val in range(2):
                    ch(nc.vector.tensor_copy(fcw[:, 16 * val:16 * val + 16].rearrange("p (r c) -> p r c", r=4),
                                             taps[:, :, bass.ds(at(FB * val, GRP).v, GRP)]))
                for j in range(GRP):
                    for val in range(2):
                        jj = 2 * j + val
                        u = at(U_FFN + jj, 12)
                        prep(u * 2 + 2)
                        prep(u * 2 + 3)
                        w3 = [fcw[:, 16 * val + 4 * r + j:16 * val + 4 * r + j + 1] for r in range(4)]
                        dst = (v_t if val else g_t)[:, :]
                        v.wait_ge(S["acc_evac"], at(U_FFN + jj + 1, 8).v)
                        ch(TS(dst, fpre[:, 2:2 + T], w3[2], w3[3], ALU.mult, ALU.add))
                        ch(STT(dst, fpre[:, 1:1 + T], w3[1], dst, ALU.mult, ALU.add))
                        ins = STT(dst, fpre[:, 0:T], w3[0], dst, ALU.mult, ALU.add)
                        if not val:
                            ins.then_inc(S["fconv_ready"], 1)
                        else:
                            ch(ins)
                            v.wait_ge(S["silu_ready"], at(j + 1, GRP).v)
                            TT(v_t[:, :], v_t[:, :], g_t[:, :], ALU.mult).then_inc(S["hidden_tmp"], 1)
                            v.wait_ge(S["hidden_hi"], at(j + 1, GRP).v)
                            TT(xs(hid_lo, j), v_t[:, :], xs(hid_hi, j).bitcast(F32), ALU.subtract)\
                                .then_inc(S["hidden_ready"], 1)
                for q in range(4):
                    u = at(U_FFN + 8 + q, 12)
                    prep(u * 2 + 2, final and q == 3)
                    prep(u * 2 + 3, final and q == 3)
                    for dt in range(4):
                        if dt < 3:
                            v.wait_ge(S["down_done"], at(3 * q + dt + 1, 12).v)
                        else:
                            v.wait_ge(S["piece_used"], (u * 2 + 2).v)
                        if q == 0 and dt == 0:
                            v.wait_ge(S["acc_zero"], 1)
                        TT(xs(accT, 4 * q + dt), xs(accT, 4 * q + dt), G[dt][:, :], ALU.add).then_inc(S["acc_added"], 1)

            with v.Fori(0, FB // GRP - 1) as i:
                ch.loop(i, 2 + 4 * (2 + 3))
                ffn(lambda b, s: Idx(b, s, i), False)
                ch.end(FB // GRP - 1)
            ffn(lambda b, s: Idx(b + s * (FB // GRP - 1)), True)
            v.wait_ge(S["r3_ready"], 1)
            for k in range(KB):
                ch(STT(xs(accT, k), xs(accT, k), g_ffn[:, k:k + 1], v_t[:, :], ALU.mult, ALU.mult))
                TT(xs(accT, k), xs(accT, k), xs(x1T, k), ALU.add).then_inc(S["fin_x"], 1)


_INS = ["x", "c", "w_ada", "b_ada", "norm_mix_pre", "norm_mix_post", "w_in", "fox_forget_bias", "fox_out_norm",
        "gdn_conv_w", "gdn_A_log", "gdn_dt_bias", "gdn_out_norm", "w_out", "norm_ffn_pre", "norm_ffn_post",
        "w_up", "ffn_conv_w", "ffn_conv_b", "w_down"]


def shape_constants():
    c = np.zeros((P, N_CONST), np.float32)
    r, k = np.arange(P)[:, None], np.arange(P)[None, :]
    c[:, C_ID:C_ID + P] = r == k
    c[:, C_ONE:C_ONE + P] = 1
    c[:, C_INC:C_INC + P] = k >= r
    c[:, C_STR:C_STR + P] = k > r
    c[:, C_NEG:C_NEG + P] = np.where(k <= r, 0.0, NEG)
    for l, b in enumerate([1] + LEVELS):
        m = (k // b == r // b + 1) & ((r // b) % 2 == 0)
        c[:, C_MU + P * l:C_MU + P * (l + 1)] = m
        if b == 1:
            c[:, C_ML1:C_ML1 + P] = m.T
    c[:, C_EPS] = EPS
    c[:, C_EPS + 1] = 1
    return c


def kernel(**inputs):
    import concourse.bacc as bacc
    from concourse.bass_utils import run_bass_kernel_spmd as run

    nc = bacc.Bacc("TRN2", target_bir_lowering=False, num_devices=1)
    arrays, args = {}, {}
    for name in _INS:
        arrays[name] = np.ascontiguousarray(inputs[name])
        args[name] = nc.dram_tensor(name, arrays[name].shape, F32, kind="ExternalInput").ap()
    arrays["consts"] = shape_constants()
    consts = nc.dram_tensor("consts", (P, N_CONST), F32, kind="ExternalInput").ap()
    out = nc.dram_tensor("out", (1, T, D), F32, kind="ExternalOutput").ap()
    build(nc, args, consts, out)
    return run(nc, [arrays], core_ids=[0]).results[0]["out"]
```
